# Optimizing a Trainium2 kernel written in Bass

```python
import math
import jax
import jax.numpy as jnp
from jax import lax
import numpy as np

D_MODEL = 1024
BATCH = 1
SEQ = 256
DEPTH = 2

MEM_LEN = 256
N_EVEN = (DEPTH + 1) // 2
N_ODD = DEPTH // 2
EPS = 1e-6
NEG_INF = -1e30

A_GROUPS = 4
A_CH = 128
A_WIDTH = A_GROUPS * A_CH
A_CHUNK = 128
B_HEADS = 8
B_KV_HEADS = 2
B_Q_PER_KV = B_HEADS // B_KV_HEADS
B_HEAD_DIM = 64
B_WIDTH = B_HEADS * B_HEAD_DIM
B_KV_WIDTH = B_KV_HEADS * B_HEAD_DIM
B_HALF_WINDOW = 128
B_BLOCK = 128
EVEN_IN = 2 * A_WIDTH + B_WIDTH + 2 * B_KV_WIDTH
EVEN_OUT = A_WIDTH + B_WIDTH
C_PAIRS = ((128, 1), (512, 4), (2048, 16))
C_GROUPS = len(C_PAIRS)
C_HEADS = 8
C_HEAD_DIM = 128
C_WIDTH = C_HEADS * C_HEAD_DIM
C_BLOCK = 64
ODD_IN = C_GROUPS * 3 * C_WIDTH
REL_BUCKETS = 32
REL_MAX_DIST = 1024
REL_HEADS = 8
X_HEADS = 4
X_HEAD_DIM = 128
X_WIDTH = X_HEADS * X_HEAD_DIM
MOE_GROUPS = 4
MOE_EPG = 4
MOE_TOP_K = 2
D_EXPERT = 512

kernel_name = 'hybrid_sgu_swa_dilated_hmoe_encoder'

def rms_norm(x, g):
    xf = x.astype(jnp.float32)
    y = xf * lax.rsqrt(jnp.mean(xf * xf, axis=-1, keepdims=True) + EPS)
    return (y * g.astype(jnp.float32)).astype(x.dtype)

def layer_norm(x, g, b):
    xf = x.astype(jnp.float32)
    mu = jnp.mean(xf, axis=-1, keepdims=True)
    var = jnp.mean(jnp.square(xf - mu), axis=-1, keepdims=True)
    y = (xf - mu) * lax.rsqrt(var + EPS)
    return (y * g.astype(jnp.float32) + b.astype(jnp.float32)).astype(x.dtype)

def t5_bucket(rel):
    nb = REL_BUCKETS // 2
    max_exact = nb // 2
    ret = jnp.where(rel > 0, nb, 0)
    n = jnp.abs(rel)
    nf = jnp.maximum(n, 1).astype(jnp.float32)
    large = max_exact + (jnp.log(nf / max_exact) / math.log(REL_MAX_DIST / max_exact)
                         * (nb - max_exact)).astype(jnp.int32)
    large = jnp.minimum(large, nb - 1)
    return ret + jnp.where(n < max_exact, n, large)

def rel_bias(table, rel):
    return jnp.moveaxis(table[t5_bucket(rel)], -1, 0).astype(jnp.float32)

def band_rel(block):
    return jnp.arange(3 * block)[None, :] - block - jnp.arange(block)[:, None]

def banded_attention(q, k, v, half, block, bias, sink=None):
    n, L, kvh, g, e = q.shape
    nb = -(-L // block)
    pad = nb * block - L
    qb = jnp.pad(q, ((0, 0), (0, pad), (0, 0), (0, 0), (0, 0))).reshape(n, nb, block, kvh, g, e)

    def windows(t):
        tp = jnp.pad(t, ((0, 0), (block, block + pad), (0, 0), (0, 0))).reshape(n, nb + 2, block, kvh, e)
        return jnp.concatenate([tp[:, :-2], tp[:, 1:-1], tp[:, 2:]], axis=2)

    kw = windows(k)
    vw = windows(v)
    qpos = jnp.arange(nb * block).reshape(nb, block)
    kpos = jnp.arange(nb)[:, None] * block - block + jnp.arange(3 * block)[None, :]
    rel = kpos[:, None, :] - qpos[:, :, None]
    valid = (jnp.abs(rel) <= half) & (kpos[:, None, :] >= 0) & (kpos[:, None, :] < L)
    logits = jnp.einsum('nbqkge,nbjke->nbkgqj', qb, kw).astype(jnp.float32) * (e ** -0.5)
    logits = logits + bias[None, None]
    logits = jnp.where(valid[None, :, None, None], logits, NEG_INF)
    m = jnp.max(logits, axis=-1)
    if sink is not None:
        s = jnp.broadcast_to(sink.astype(jnp.float32)[None, None, :, :, None], m.shape)
        m = jnp.maximum(m, s)
    p = jnp.exp(logits - m[..., None])
    den = jnp.sum(p, axis=-1)
    if sink is not None:
        den = den + jnp.exp(s - m)
    out = jnp.einsum('nbkgqj,nbjke->nbqkge', p, vw.astype(jnp.float32))
    out = out / jnp.moveaxis(den, -1, 2)[..., None]
    out = out.reshape(n, nb * block, kvh, g, e)[:, :L].astype(q.dtype)
    lse = jnp.moveaxis(m + jnp.log(den), -1, 2).reshape(n, nb * block, kvh, g)[:, :L]
    return out, lse

def spatial_gating(u, v, ln_g, ln_b, w_s, b_s):
    bsz, s, _ = v.shape
    vn = layer_norm(v, ln_g, ln_b).reshape(bsz, s // A_CHUNK, A_CHUNK, A_GROUPS, A_CH)
    mixed = jnp.einsum('gpq,bnqgc->bnpgc', w_s, vn) + jnp.transpose(b_s)[None, None, :, :, None]
    return u * mixed.reshape(bsz, s, A_WIDTH).astype(u.dtype)

def even_mixer(h, w_in, w_out, ln_g, ln_b, w_s, b_s, sink, table):
    bsz, s, _ = h.shape
    z = h @ w_in
    u, va, q, k, v = jnp.split(z, [A_WIDTH, 2 * A_WIDTH, 2 * A_WIDTH + B_WIDTH,
                                   2 * A_WIDTH + B_WIDTH + B_KV_WIDTH], axis=-1)
    ya = spatial_gating(jax.nn.gelu(u), jax.nn.gelu(va), ln_g, ln_b, w_s, b_s)
    q = q.reshape(bsz, s, B_KV_HEADS, B_Q_PER_KV, B_HEAD_DIM)
    k = k.reshape(bsz, s, B_KV_HEADS, B_HEAD_DIM)
    v = v.reshape(bsz, s, B_KV_HEADS, B_HEAD_DIM)
    bias = rel_bias(table, band_rel(B_BLOCK)).reshape(B_KV_HEADS, B_Q_PER_KV, B_BLOCK, 3 * B_BLOCK)
    yb, _ = banded_attention(q, k, v, B_HALF_WINDOW, B_BLOCK, bias,
                             sink.reshape(B_KV_HEADS, B_Q_PER_KV))
    yb = yb.reshape(bsz, s, B_WIDTH)
    return jnp.concatenate([ya, yb], axis=-1) @ w_out

def odd_mixer(h, w_in, w_out, table):
    bsz, s, _ = h.shape
    z = (h @ w_in).reshape(bsz, s, C_GROUPS, 3, C_HEADS, C_HEAD_DIM)
    outs = []
    lses = []
    for gi, (window, dil) in enumerate(C_PAIRS):
        half = window // 2 // dil
        length = s // dil

        def strided(t):
            return t.reshape(bsz, length, dil, C_HEADS, C_HEAD_DIM).transpose(0, 2, 1, 3, 4).reshape(
                bsz * dil, length, C_HEADS, C_HEAD_DIM)

        qs = strided(z[:, :, gi, 0])[:, :, :, None]
        bias = rel_bias(table, band_rel(C_BLOCK) * dil)[:, None]
        o, lse = banded_attention(qs, strided(z[:, :, gi, 1]), strided(z[:, :, gi, 2]), half, C_BLOCK, bias)
        o = o[:, :, :, 0].reshape(bsz, dil, length, C_HEADS, C_HEAD_DIM).transpose(0, 2, 1, 3, 4)
        outs.append(o.reshape(bsz, s, C_HEADS, C_HEAD_DIM))
        lse = lse[..., 0].reshape(bsz, dil, length, C_HEADS).transpose(0, 2, 1, 3)
        lses.append(lse.reshape(bsz, s, C_HEADS))
    wts = jax.nn.softmax(jnp.stack(lses, axis=0), axis=0)
    y = jnp.einsum('gbsh,gbshe->bshe', wts, jnp.stack(outs, axis=0).astype(jnp.float32))
    return y.reshape(bsz, s, C_WIDTH).astype(h.dtype) @ w_out

def cross_attention(h, mem_n, wq, wkv, wo):
    bsz, s, _ = h.shape
    q = (h @ wq).reshape(bsz, s, X_HEADS, X_HEAD_DIM)
    kv = (mem_n @ wkv).reshape(bsz, mem_n.shape[1], 2, X_HEADS, X_HEAD_DIM)
    logits = jnp.einsum('bshe,bmhe->bhsm', q, kv[:, :, 0]).astype(jnp.float32) * (X_HEAD_DIM ** -0.5)
    p = jax.nn.softmax(logits, axis=-1)
    o = jnp.einsum('bhsm,bmhe->bshe', p, kv[:, :, 1].astype(jnp.float32)).astype(h.dtype)
    return o.reshape(bsz, s, X_WIDTH) @ wo

def hier_moe(h, w_grp, b_grp, w_exp, b_exp, w_gate, w_up, w_down):
    bsz, s, d = h.shape
    t = h.reshape(-1, d)
    g_logits = (t @ w_grp).astype(jnp.float32) + b_grp.astype(jnp.float32)
    g_prob = jax.nn.softmax(g_logits, axis=-1)
    grp = jnp.argmax(g_logits, axis=-1)
    g_gate = jnp.take_along_axis(g_prob, grp[:, None], axis=-1)
    e_logits = jnp.einsum('td,dge->tge', t, w_exp).astype(jnp.float32) + b_exp.astype(jnp.float32)
    e_sel = jnp.take_along_axis(e_logits, grp[:, None, None], axis=1)[:, 0]
    top_v, top_i = lax.top_k(e_sel, MOE_TOP_K)
    top_w = jax.nn.softmax(top_v, axis=-1)
    within = jnp.sum(jax.nn.one_hot(top_i, MOE_EPG, dtype=jnp.float32) * top_w[..., None], axis=1)
    gate = jax.nn.one_hot(grp, MOE_GROUPS, dtype=jnp.float32)[:, :, None] * (g_gate * within)[:, None, :]
    y = jnp.zeros((t.shape[0], d), jnp.float32)
    for gi in range(MOE_GROUPS):
        hid = jax.nn.silu(jnp.einsum('td,edf->tef', t, w_gate[gi])) * jnp.einsum('td,edf->tef', t, w_up[gi])
        hid = hid * gate[:, gi, :, None]
        y = y + jnp.einsum('tef,efd->td', hid, w_down[gi])
    return y.reshape(bsz, s, d).astype(h.dtype)

def setup_inputs(seed: int = 0) -> dict:
    key = jax.random.key(seed)
    ks = jax.random.split(key, 27)
    f32 = jnp.float32

    def nrm(k, shape, scale):
        return jax.random.normal(k, shape, f32) * scale

    def gain(k, shape):
        return 1.0 + 0.02 * jax.random.normal(k, shape, f32)

    d = D_MODEL
    return {
        'x': nrm(ks[0], (BATCH, SEQ, d), 1.0),
        'mem': nrm(ks[1], (BATCH, MEM_LEN, d), 1.0),
        'ln_mix': gain(ks[2], (DEPTH, d)),
        'ln_cross': gain(ks[3], (DEPTH, d)),
        'ln_mem': gain(ks[4], (DEPTH, d)),
        'ln_ffn': gain(ks[5], (DEPTH, d)),
        'ln_final': gain(ks[6], (d,)),
        'rel_table': nrm(ks[7], (REL_BUCKETS, REL_HEADS), 0.5),
        'even_w_in': nrm(ks[8], (N_EVEN, d, EVEN_IN), d ** -0.5),
        'even_w_out': nrm(ks[9], (N_EVEN, EVEN_OUT, d), EVEN_OUT ** -0.5),
        'sgu_ln_g': gain(ks[10], (N_EVEN, A_WIDTH)),
        'sgu_ln_b': nrm(ks[11], (N_EVEN, A_WIDTH), 0.02),
        'sgu_w': nrm(ks[12], (N_EVEN, A_GROUPS, A_CHUNK, A_CHUNK), A_CHUNK ** -0.5),
        'sgu_b': 1.0 + nrm(ks[13], (N_EVEN, A_GROUPS, A_CHUNK), 0.02),
        'attn_sink': nrm(ks[14], (N_EVEN, B_HEADS), 0.5),
        'odd_w_in': nrm(ks[15], (N_ODD, d, ODD_IN), d ** -0.5),
        'odd_w_out': nrm(ks[16], (N_ODD, C_WIDTH, d), C_WIDTH ** -0.5),
        'xq_w': nrm(ks[17], (DEPTH, d, X_WIDTH), d ** -0.5),
        'xkv_w': nrm(ks[18], (DEPTH, d, 2 * X_WIDTH), d ** -0.5),
        'xo_w': nrm(ks[19], (DEPTH, X_WIDTH, d), X_WIDTH ** -0.5),
        'router_group_w': nrm(ks[20], (DEPTH, d, MOE_GROUPS), d ** -0.5),
        'router_group_b': nrm(ks[21], (DEPTH, MOE_GROUPS), 0.01),
        'router_expert_w': nrm(ks[22], (DEPTH, d, MOE_GROUPS, MOE_EPG), d ** -0.5),
        'router_expert_b': nrm(ks[23], (DEPTH, MOE_GROUPS, MOE_EPG), 0.01),
        'expert_w_gate': nrm(ks[24], (DEPTH, MOE_GROUPS, MOE_EPG, d, D_EXPERT), d ** -0.5),
        'expert_w_up': nrm(ks[25], (DEPTH, MOE_GROUPS, MOE_EPG, d, D_EXPERT), d ** -0.5),
        'expert_w_down': nrm(ks[26], (DEPTH, MOE_GROUPS, MOE_EPG, D_EXPERT, d), D_EXPERT ** -0.5),
    }

def reference(x, mem, ln_mix, ln_cross, ln_mem, ln_ffn, ln_final, rel_table,
              even_w_in, even_w_out, sgu_ln_g, sgu_ln_b, sgu_w, sgu_b, attn_sink,
              odd_w_in, odd_w_out, xq_w, xkv_w, xo_w,
              router_group_w, router_group_b, router_expert_w, router_expert_b,
              expert_w_gate, expert_w_up, expert_w_down):
    h = x
    for layer in range(DEPTH):
        i = layer // 2
        n = rms_norm(h, ln_mix[layer])
        if layer % 2 == 0:
            mix = even_mixer(n, even_w_in[i], even_w_out[i], sgu_ln_g[i], sgu_ln_b[i],
                             sgu_w[i], sgu_b[i], attn_sink[i], rel_table)
        else:
            mix = odd_mixer(n, odd_w_in[i], odd_w_out[i], rel_table)
        h = h + mix.astype(h.dtype)
        mem_n = rms_norm(mem, ln_mem[layer])
        h = h + cross_attention(rms_norm(h, ln_cross[layer]), mem_n, xq_w[layer], xkv_w[layer], xo_w[layer])
        h = h + hier_moe(rms_norm(h, ln_ffn[layer]), router_group_w[layer], router_group_b[layer],
                         router_expert_w[layer], router_expert_b[layer],
                         expert_w_gate[layer], expert_w_up[layer], expert_w_down[layer])
    return rms_norm(h, ln_final)


_drawn_inputs = setup_inputs


def setup_inputs(seed=0):
    import zlib

    import numpy as np

    out = dict(_drawn_inputs(seed))
    spreads = {}
    factors = {'ln_cross': 2.992,
     'ln_final': 2.736,
     'attn_sink': 8.0,
     'router_group_b': 8.0,
     'router_expert_b': 4.545}
    for name, (base, spread) in spreads.items():
        noise = np.random.default_rng([zlib.crc32(name.encode()), seed]).standard_normal(out[name].shape)
        drawn = base * np.exp(spread * noise) if base else spread * noise
        out[name] = jnp.asarray(drawn.astype(out[name].dtype))
    for name, factor in factors.items():
        out[name] = (out[name] * factor).astype(out[name].dtype)
    return out
```

```python
from contextlib import ExitStack

import numpy as np

import concourse.bass as bass
from concourse import mybir

F32 = mybir.dt.float32
I32 = mybir.dt.int32
ALU = mybir.AluOpType
ACT = mybir.ActivationFunctionType
AX = mybir.AxisListType

P = 128
D = 1024
SEQ = 256
MEM = 256
DEPTH = 2
TILES = SEQ // P
CH = D // P
EPS = 1e-6
MASKED = -1e30

A_GROUPS = 4
A_WIDTH = 512
B_HEADS = 8
B_DIM = 64
B_HALF = 128
C_HEADS = 8
C_PAIRS = ((128, 1), (512, 4), (2048, 16))
CG = len(C_PAIRS)
X_HEADS = 4
BUCKETS = 32
MAX_DIST = 1024
GROUPS = 4
EPG = 4
NR = GROUPS + GROUPS * EPG
FE = 512
FC = FE // P

RING = 6
SLOT = 4096
SPAN = 512
SKEW = 32
BROW = (SKEW + 1) * SPAN
SCRATCH = 15616

RSQRT_FACTOR = -1.0 / 8192.0
MAGIC = float(0x5F3759DF)


def bucket(rel):
    half = BUCKETS // 2
    exact = half // 2
    n = abs(rel)
    if n < exact:
        b = n
    else:
        b = min(exact + int(np.log(n / exact) / np.log(MAX_DIST / exact) * (half - exact)), half - 1)
    return b + (half if rel > 0 else 0)


def bias_selectors():
    e = np.zeros((BUCKETS + 1, 1 + CG, SPAN), np.float32)
    for i in range(SPAN):
        d = i - SPAN // 2
        allowed = [abs(d) <= B_HALF] + [d % dil == 0 and abs(d) // dil <= window // 2 // dil
                                        for window, dil in C_PAIRS]
        for m, ok in enumerate(allowed):
            e[bucket(d) if ok else BUCKETS, m, i] = 1.0
    return e


def constants():
    c = np.zeros((P, 4 * P + 8), np.float32)
    c[:, 0:P] = np.eye(P)
    c[:, P:2 * P] = np.triu(np.ones((P, P)), 1)
    c[:, 2 * P:3 * P] = np.arange(1, P + 1)[None, :]
    c[:, 3 * P:4 * P] = 1.0
    c[:, 4 * P:] = np.array([4, 3, 2, 1] * 2)[None, :]
    return c


def encoder(nc, x, mem, ln_mix, ln_cross, ln_mem, ln_ffn, ln_final, rel_table, even_w_in, even_w_out,
            sgu_ln_g, sgu_ln_b, sgu_w, sgu_b, attn_sink, odd_w_in, odd_w_out, xq_w, xkv_w, xo_w,
            router_group_w, router_group_b, router_expert_w, router_expert_b,
            expert_w_gate, expert_w_up, expert_w_down, consts, selectors, out):
    with ExitStack() as ctx:
        def sb(name, shape, dt=F32):
            return ctx.enter_context(nc.sbuf_tensor(name, shape, dt))

        def sem(name):
            return ctx.enter_context(nc.semaphore(name))

        ring = sb("ring", [P, RING, SLOT])
        h = sb("h", [P, TILES, D])
        nrm = sb("nrm", [P, TILES, CH, P])
        nT = sb("nT", [P, CH, SEQ])
        xkT = sb("xkT", [P, DEPTH, X_HEADS, MEM])
        xv = sb("xv", [P, DEPTH, TILES, X_HEADS * P])
        cst = sb("cst", [P, 4 * P + 8])
        gmix = sb("gmix", [P, DEPTH, CH])
        gcross = sb("gcross", [P, DEPTH, CH])
        gmem = sb("gmem", [P, DEPTH, CH])
        gffn = sb("gffn", [P, DEPTH, CH])
        rw = sb("rw", [P, DEPTH, CH, NR])
        rb = sb("rb", [P, DEPTH, NR])
        sink = sb("sink", [P, B_HEADS])
        tab = sb("tab", [BUCKETS + 1, B_HEADS])
        ssq = sb("ssq", [P, TILES + 1])
        var = sb("var", [P, TILES])
        seed = sb("seed", [P, TILES], I32)
        rst = sb("rst", [P, TILES])
        tmp = sb("tmp", [P, TILES])
        mx = sb("mx", [P, 2, TILES])
        negm = sb("negm", [P, 2, TILES])
        den = sb("den", [P, 2, TILES])
        esink = sb("esink", [P, 2, TILES])
        rden = sb("rden", [P, 2, TILES])
        stats = sb("stats", [P, TILES, 6])
        aggr = sb("aggr", [P, TILES, 2])
        ovf = sb("ovf", [P, DEPTH, 2], I32)
        scratch = sb("scratch", [P, SCRATCH])

        ident = cst[:, 0:P]
        earlier = cst[:, P:2 * P]
        slotno = cst[:, 2 * P:3 * P]
        ones = cst[:, 3 * P:4 * P]
        first4 = cst[:, 4 * P:4 * P + 8].rearrange("p (t g) -> p t g", t=TILES)

        class Area:
            def __init__(self):
                self.at = 0

            def take(self, n):
                self.at += n
                assert self.at <= SCRATCH
                return scratch[:, self.at - n:self.at]

        a = Area()
        q4 = a.take(4 * SEQ).rearrange("p (b s) -> p b s", b=4)
        prob = a.take(2 * 2 * 256).rearrange("p (n t k) -> p n t k", n=2, t=2)
        probT = a.take(2 * 2 * 256).rearrange("p (n b q) -> p n b q", n=2, b=2)
        yT = a.take(8 * SEQ).rearrange("p (j s) -> p j s", j=8)
        mT1 = a.take(CH * MEM).rearrange("p (c m) -> p c m", c=CH)
        tbias = a.take(B_HEADS * 384).rearrange("p (h x) -> p h x", h=B_HEADS)
        va = a.take(TILES * A_WIDTH).rearrange("p (t c) -> p t c", t=TILES)
        uT = a.take(A_GROUPS * SEQ).rearrange("p (g s) -> p g s", g=A_GROUPS)
        kTe = a.take(2 * SEQ).rearrange("p (n s) -> p n s", n=2)
        ve = a.take(SEQ).rearrange("p (t c) -> p t c", t=TILES)
        sguw = a.take(4 * P).rearrange("p (g q) -> p g q", g=4)
        wsT = a.take(4 * P).rearrange("p (g q) -> p g q", g=4)
        lng = a.take(A_WIDTH)
        lnb = a.take(A_WIDTH)
        sgub = a.take(4 * P).rearrange("p (g q) -> p g q", g=4)
        mem_rows = scratch[:, 0:TILES * D].rearrange("p (t d) -> p t d", t=TILES)
        vec = yT
        sel33 = va

        a = Area()
        hb = a.take(2 * CG * 384).rearrange("p (n g x) -> p n g x", n=2, g=CG)
        oq = a.take(CG * SEQ).rearrange("p (g s) -> p g s", g=CG)
        ok = a.take(CG * SEQ).rearrange("p (g s) -> p g s", g=CG)
        ov = a.take(2 * TILES * CG * P).rearrange("p (n t c) -> p n t c", n=2, t=TILES)
        op = a.take(CG * 2 * 256).rearrange("p (g t k) -> p g t k", g=CG, t=2)
        opT = a.take(CG * 2 * 256).rearrange("p (g b q) -> p g b q", g=CG, b=2)
        oyT = a.take(C_HEADS * SEQ).rearrange("p (j s) -> p j s", j=C_HEADS)

        a = Area()
        xg = a.take(GROUPS * CH * P).rearrange("p (g c s) -> p g c s", g=GROUPS, c=CH)
        xcur = a.take(CH * P).rearrange("p (c s) -> p c s", c=CH)
        silu = a.take(2 * FE).rearrange("p (n f) -> p n f", n=2)
        hid = a.take(FE).rearrange("p (c f) -> p c f", c=FC)
        hidT = a.take(FE).rearrange("p (c s) -> p c s", c=FC)
        ysb = a.take(GROUPS * D).rearrange("p (g d) -> p g d", g=GROUPS)
        sel = a.take(TILES * GROUPS * P).rearrange("p (t g s) -> p t g s", t=TILES, g=GROUPS)
        selT = a.take(GROUPS * SEQ).rearrange("p (g s) -> p g s", g=GROUPS)
        gslot = a.take(GROUPS * EPG).rearrange("p (g e) -> p g e", g=GROUPS)
        gcur = a.take(EPG)
        lg = a.take(TILES * NR).rearrange("p (t n) -> p t n", t=TILES)

        def small(*dims):
            n = TILES
            for d in dims:
                n *= d
            v = a.take(n)
            if dims == ():
                return v
            if len(dims) == 1:
                return v.rearrange("p (t n) -> p t n", t=TILES)
            return v.rearrange("p (t g e) -> p t g e", t=TILES, g=dims[0])

        gm, gsum, ggate, mw, m1, m2, ex2, w1, w2 = (small() for _ in range(9))
        gd, eg, eq, oh, esel, oh1, e2, oh2, gate, gate2, key = (small(4) for _ in range(11))
        prod = small(4, 4)
        over = a.take(GROUPS)
        ovd = a.take(GROUPS)
        ovn = a.take(2)
        key2 = small()

        wa = xg.rearrange("p g c s -> p (g c s)")
        wb = ysb.rearrange("p g d -> p (g d)")
        acc2 = sel.rearrange("p t g s -> p (t g s)")
        sel2 = a.take(TILES * P).rearrange("p (t s) -> p t s", t=TILES)

        lnf = scratch[:, 0:D]

        bank = [ctx.enter_context(nc.psum_tensor(f"bank{i}", [P, 512], F32)) for i in range(8)]

        def scatter_bank(i):
            return bank[(5, 0, 1, 2)[i]]

        biasd = nc.dram_tensor("bias_rows", [1 + CG, B_HEADS * BROW], F32, kind="Internal").ap()

        landed = [sem(f"weights_landed{i}") for i in range(RING)]
        ring_used = sem("ring_slots_used")
        mem_in = sem("mem_loaded")
        x_in = sem("x_loaded")
        id_in = sem("constants_loaded")
        gmem_in = sem("memory_gain_loaded")
        cst_in = sem("bias_table_loaded")
        par_in = sem("parameters_loaded")
        lnf_in = sem("final_gain_loaded")
        tab_set = sem("table_mask_row_set")
        vec_ps = sem("bias_rows_in_psum")
        vec_sb = sem("bias_rows_in_sbuf")
        bias_out = sem("bias_rows_in_dram")
        tbias_in = sem("layer0_bias_loaded")
        hb_in = [sem(f"head_bias_loaded{i}") for i in range(2)]
        ssq_act = sem("tile0_squares_summed")
        rstd_set = sem("rstd_ready")
        nrm0 = sem("tile0_normalised")
        nrm1a = sem("tile1_first_half_normalised")
        nrm1 = sem("tile1_second_half_normalised")
        piece_ready = sem("piece_in_psum")
        evac = [sem("bank6_evacuated"), sem("bank7_evacuated")]
        dve_step = sem("vector_step_done")
        scores = sem("scores_in_psum")
        maxed = sem("row_max_ready")
        exped = sem("exponentials_ready")
        probs = sem("probabilities_ready")
        pT_ps = sem("probabilities_transposed")
        pT_sb = sem("transposed_probabilities_in_sbuf")
        pv_ps = sem("head_output_in_psum")
        pv_sb = sem("head_output_in_sbuf")
        o_scores = sem("dilated_scores_in_psum")
        o_logits = sem("dilated_logits_in_sbuf")
        o_maxed = sem("dilated_row_max_ready")
        o_exped = sem("dilated_exponentials_ready")
        o_rden = sem("dilated_row_sums_inverted")
        o_probs = sem("dilated_probabilities_ready")
        o_pT_ps = sem("dilated_probabilities_transposed")
        o_pT_sb = sem("dilated_transposed_in_sbuf")
        o_pv_ps = sem("dilated_output_in_psum")
        o_pv_sb = sem("dilated_output_in_sbuf")
        vn_set = sem("gated_values_normalised")
        ya_set = sem("gated_output_ready")
        proj = sem("projection_in_psum")
        resid = sem("residual_updated")
        r_in = sem("router_exponents_in")
        r_exp = sem("router_exponentials_ready")
        oh_set = sem("group_onehot_ready")
        sel_set = sem("slot_selectors_ready")
        gate_ps = sem("gate_products_in_psum")
        silu_sb = sem("silu_in_sbuf")
        up_ps = sem("up_products_in_psum")
        hid_sb = sem("hidden_rows_ready")
        hT_ps = sem("hidden_transposed")
        hT_sb = sem("hidden_transposed_in_sbuf")
        y_ps = sem("group_output_in_psum")
        y_free = sem("output_banks_free")
        xcur_set = sem("group_tokens_ready")
        moe_done = sem("expert_layer_done")
        ovf_set = sem("overflow_flag_set")
        SECOND = ("sel", "parts", "tokens", "gate_in", "up_in", "down_in", "gate_ps", "up_ps", "silu", "hid",
                  "hT_ps", "hT_sb", "y_ps", "y_sb", "proj", "step")
        second = [{n: sem(f"second_pass{l}_{n}") for n in SECOND} for l in range(DEPTH)]
        fin_set = sem("output_rows_ready")
        out_done = sem("output_stored")

        block = ctx.enter_context(nc.Block())

        W_K0, W_V0, W_VA, W_Q, W_KV, W_U, W_OA, W_OB, W_XQ0, W_K1, W_XO0, W_V1 = range(12)
        W_MOE0 = 12
        PER_GROUP = 3 * EPG
        W_ODD = W_MOE0 + GROUPS * PER_GROUP
        W_OO = W_ODD + 3 * C_HEADS
        W_XQ1 = W_OO + 2
        W_XO1 = W_XQ1 + 1
        W_MOE1 = W_XO1 + 1
        W_MOE = [W_MOE0, W_MOE1]
        W_XQ = [W_XQ0, W_XQ1]
        W_XO = [W_XO0, W_XO1]

        def slot(n):
            return ring[:, n % RING, :]

        PARTS = {W_ODD + i: CG for i in range(3 * C_HEADS)}
        landed_at, level = [], [0] * RING
        for i in range(W_MOE1 + GROUPS * PER_GROUP):
            level[i % RING] += 16 * PARTS.get(i, 1)
            landed_at.append(level[i % RING])

        def arrived(eng, n, later=0):
            eng.wait_ge(landed[n % RING], landed_at[n] + later)

        PIECES = {}

        def number(*names):
            for n in names:
                PIECES[n] = len(PIECES)

        number(*[f"nm{j}" for j in range(4)], "k0a", "k0b", "v0a", "v0b", *[f"n1{j}" for j in range(4)],
               "va0", "va1", "q0", "q1", "kv", "wsT", "u0", "u1", "mix0", "mix1", "k1a",
               *[f"n2{j}" for j in range(4)], "xq0a", "xq0b", "k1b", "v1a", *[f"n3{j}" for j in range(4)])

        def number_moe(l):
            number(f"router{l}", *["v1b"] * (l == 0), f"pos{l}", *[f"gather{l}{c}" for c in range(CH)], f"gates{l}",
                   f"selT{l}0", f"selT{l}1")

        number_moe(0)
        number(*[f"n4{j}" for j in range(4)])
        ODD0 = len(PIECES)
        number(*[f"odd{i}" for i in range(5 * C_HEADS)])
        number(*[f"n5{j}" for j in range(4)], "xq1a", "xq1b", *[f"n6{j}" for j in range(4)])
        number_moe(1)

        def k_of(name):
            return PIECES[name] if isinstance(name, str) else name

        def pbank(name):
            return bank[6 + k_of(name) % 2]

        def piece_free(eng, name, rounds=0):
            k = k_of(name)
            if k >= 2:
                eng.wait_ge(evac[k % 2], k // 2 + rounds)

        def piece_in(eng, name, rounds=0):
            eng.wait_ge(piece_ready, k_of(name) + 1 + rounds * 2)

        def piece_out(eng, name, rounds=0):
            k = k_of(name)
            eng.wait_ge(evac[k % 2], k // 2 + 1 + rounds)

        R_MIX0, R_X0, R_MOE0, R_MIX1, R_X1, R_MOE1 = (4 * i for i in range(6))
        NORM_AFTER = {"1": None, "2": R_MIX0 + 4, "3": R_X0 + 4, "4": R_MOE0 + 4, "5": R_MIX1 + 4, "6": R_X1 + 4,
                      "7": R_MOE1 + 4}
        NORM_SEQ = {"m": 0, "1": 1, "2": 2, "3": 3, "4": 4, "5": 5, "6": 6, "7": 7}
        A_EVEN, A_X = 0, [B_HEADS, B_HEADS + X_HEADS]

        def wrows(w):
            return w.rearrange("(p c) n -> p c n", c=CH)

        def skewed(rows, a, first=0, worked_out=lambda at: at):
            at = worked_out(first + P - SKEW * a)
            return rows[:, bass.ds(at, SKEW * (SPAN - 1))].rearrange("h (r x) -> r h x", x=SPAN - 1)[:, :, 0:384]

        @block.sync
        def _(sp):
            def load(n, dst, src, turns=0):
                if n >= RING:
                    sp.wait_ge(ring_used, n - RING + 1 + turns * RING)
                sp.dma_start(dst, src).then_inc(landed[n % RING], 16)

            def worked_out(at):
                return at if isinstance(at, int) else sp.snap(at)

            def full(n):
                return slot(n).rearrange("p (c n) -> p c n", c=CH)

            sp.dma_start(cst[:, :], consts).then_inc(id_in, 16)
            sp.dma_start(mem_rows, mem[0].rearrange("(t p) d -> p t d", p=P)).then_inc(mem_in, 16)
            load(W_K0, full(W_K0), wrows(xkv_w[0])[:, :, 0:512])
            sp.dma_start(h[:, :, :], x[0].rearrange("(t p) d -> p t d", p=P)).then_inc(x_in, 16)
            load(W_V0, full(W_V0), wrows(xkv_w[0])[:, :, 512:1024])
            win = wrows(even_w_in[0])
            load(W_VA, full(W_VA), win[:, :, A_WIDTH:2 * A_WIDTH])
            load(W_Q, full(W_Q), win[:, :, 2 * A_WIDTH:2 * A_WIDTH + 512])
            load(W_KV, slot(W_KV)[:, 0:CH * 256].rearrange("p (c n) -> p c n", c=CH), win[:, :, 1536:1792])
            load(W_U, full(W_U), win[:, :, 0:A_WIDTH])
            for k in range(2):
                load(W_OA + k, slot(W_OA + k).rearrange("p (j n) -> p j n", j=4),
                     even_w_out[0, 512 * k:512 * k + 512].rearrange("(j p) n -> p j n", p=P))

            def cross(l):
                load(W_XQ[l], full(W_XQ[l]), wrows(xq_w[l]), 0)
                if l == 0:
                    load(W_K1, full(W_K1), wrows(xkv_w[1])[:, :, 0:512])
                load(W_XO[l], slot(W_XO[l]).rearrange("p (j n) -> p j n", j=4),
                     xo_w[l].rearrange("(j p) n -> p j n", p=P), 0)
                if l == 0:
                    load(W_V1, full(W_V1), wrows(xkv_w[1])[:, :, 512:1024])

            def experts(l):
                base = W_MOE[l]

                def w(kind, g, e):
                    src = {"g": expert_w_gate, "u": expert_w_up, "d": expert_w_down}[kind]
                    flat = src.rearrange("l g e d f -> (l g e d f)")
                    at = worked_out(g + (l * GROUPS * EPG + e - 2 * EPG) * D * FE)
                    return flat[bass.ds(at, D * FE)].rearrange("(p n) -> p n", p=P)

                load(base, slot(base), w("g", 2 * EPG * D * FE, 0))
                load(base + 1, slot(base + 1), w("u", 2 * EPG * D * FE, 0))

                def group(g, last, turns):
                    n = base + 2
                    for e in range(EPG):
                        if e + 1 < EPG:
                            order = [("g", g, e + 1), ("u", g, e + 1), ("d", g, e)]
                        elif not last:
                            order = [("g", g, EPG), ("u", g, EPG), ("d", g, e)]
                        else:
                            order = [("d", g, e)]
                        for kind, gg, ee in order:
                            load(n, slot(n), w(kind, gg, ee), turns)
                            n += 1

                with sp.Fori(2, GROUPS + 1) as g:
                    group(g * (EPG * D * FE), False, (g - 2) * (PER_GROUP // RING))
                group((GROUPS + 1) * EPG * D * FE, True, (GROUPS - 1) * (PER_GROUP // RING))

            cross(0)
            experts(0)

            def head_weights(hd, n, turns=0):
                w = odd_w_in[0].rearrange("(p c) (g w n) -> p c g w n", c=CH, g=CG, w=3)
                hd = worked_out(hd)
                for which in range(3):
                    if n + which >= RING:
                        sp.wait_ge(ring_used, n + which - RING + 1 + turns * RING)
                    dst = slot(n + which)[:, 0:CH * CG * P].rearrange("p (c g e) -> p c g e", c=CH, g=CG)
                    for g in range(CG):
                        sp.dma_start(dst[:, :, g, :], w[:, :, g, which, bass.ds(hd, P)]).then_inc(landed[(n + which) % RING], 16)

            def head_bias_parts(row):
                return [skewed(biasd[1:1 + CG], a, row, worked_out) for a in range(P // SKEW)]

            def head_bias(parts, n):
                for a, part in enumerate(parts):
                    sp.dma_start(hb[SKEW * a:SKEW * (a + 1), n], part).then_inc(hb_in[n], 16)

            head_weights(0, W_ODD)
            sp.wait_ge(bias_out, 16 * (1 + CG))
            sp.wait_ge(moe_done, 1)
            head_bias(head_bias_parts(0), 0)
            head_bias(head_bias_parts(BROW), 1)
            with sp.Fori(0, C_HEADS // 2 - 1) as j:
                column = sp.snap(j * (2 * P))
                row = sp.snap(j * (2 * BROW))
                head_weights(column + P, W_ODD + 3, j)
                head_weights(column + 2 * P, W_ODD + 6, j)
                for n in range(2):
                    parts = head_bias_parts(row + (2 + n) * BROW)
                    sp.wait_ge(o_maxed, n + 1 + j * 2)
                    head_bias(parts, n)
            head_weights((C_HEADS - 1) * P, W_ODD + 3, C_HEADS // 2 - 1)
            for k in range(2):
                load(W_OO + k, slot(W_OO + k).rearrange("p (j n) -> p j n", j=4),
                     odd_w_out[0, 512 * k:512 * k + 512].rearrange("(j p) n -> p j n", p=P))
            cross(1)
            experts(1)
            for t in range(TILES):
                sp.wait_ge(fin_set, t + 1)
                sp.dma_start(out[0, t * P:(t + 1) * P, :], nrm[:, t].rearrange("p c q -> p (c q)")).then_inc(out_done, 16)
            sp.wait_ge(out_done, 16 * TILES)

        NORMS = {
            "m": (mem_rows, [(gmem[:, 0], nT), (gmem[:, 1], mT1)]),
            "1": (h, [(gmix[:, 0], nT)]), "2": (h, [(gcross[:, 0], nT)]), "3": (h, [(gffn[:, 0], nT)]),
            "4": (h, [(gmix[:, 1], nT)]), "5": (h, [(gcross[:, 1], nT)]), "6": (h, [(gffn[:, 1], nT)]),
            "7": (h, []),
        }

        AFTER = {"2": R_MIX0, "3": R_X0, "5": R_MIX1, "6": R_X1}

        def norm_source_ready(eng, name):
            if name == "m":
                eng.wait_ge(mem_in, 16)
            elif name == "1":
                eng.wait_ge(x_in, 16)
                piece_in(eng, "nm3")
            elif name in "47":
                eng.wait_ge(moe_done, {"4": 1, "7": 2}[name])
            else:
                eng.wait_ge(resid, AFTER[name] + 2)

        FILL = ["wsT", "u0", None, "u1", None, "mix0", None, "mix1", None, None]

        BEFORE = {"2": "k1a", "3": "v1a"}

        def evacuate_filler(eng, is_act, name):
            if name == "wsT":
                evacuate(eng, is_act, name, two(wsT))
            elif name in ("u0", "u1"):
                i = int(name[1])
                evacuate(eng, is_act, name, two(uT[:, 2 * i:2 * i + 2]), func=ACT.Gelu_apprx_tanh)
            elif name in ("k1a", "k1b"):
                i = "ab".index(name[2])
                evacuate(eng, is_act, name, two(xkT[:, 1, 2 * i:2 * i + 2]))
            elif name in ("v1a", "v1b"):
                evacuate(eng, is_act, name, xv[:, 1, "ab".index(name[2]), :])

        def evacuate_norm(eng, is_act, name):
            if name in BEFORE:
                evacuate_filler(eng, is_act, BEFORE[name])
            if name == "m":
                eng.wait_ge(gmem_in, 16)
            elif name == "1":
                eng.wait_ge(par_in, PARAMS)
            for j in range(4):
                k = PIECES[f"n{name}{j}"]
                if (k % 2 == 1) != is_act:
                    continue
                piece_in(eng, k)
                for i in range(2):
                    c = 2 * j + i
                    for gain, dst in NORMS[name][1]:
                        src = pbank(k)[:, i * SEQ:(i + 1) * SEQ]
                        if is_act:
                            last = nc.scalar.activation(dst[:, c, :], src, ACT.Copy, scale=gain[:, c:c + 1])
                        else:
                            last = nc.vector.tensor_scalar(dst[:, c, :], src, gain[:, c:c + 1], None, ALU.mult)
                last.then_inc(evac[k % 2], 1)

        def rows(t):
            return nrm[:, t].rearrange("p c q -> p (c q)")

        PARAMS = 16 * 16
        BY_ACT = {"va0", "va1", "u0", "u1", "v1b"}

        def by_act(name):
            return name in BY_ACT or PIECES[name] % 2 == 1

        def evacuate(eng, is_act, name, dst, src=None, func=None):
            if by_act(name) != is_act:
                return
            piece_in(eng, name)
            src = pbank(name)[:, :] if src is None else src
            if is_act:
                nc.scalar.activation(dst, src, func or ACT.Copy).then_inc(evac[PIECES[name] % 2], 1)
            else:
                nc.vector.tensor_copy(dst, src).then_inc(evac[PIECES[name] % 2], 1)

        def two(v):
            return v.rearrange("p b s -> p (b s)")

        def evacuate_kv(eng, is_act, l):
            for i in range(2):
                evacuate(eng, is_act, f"k{l}{'ab'[i]}", two(xkT[:, l, 2 * i:2 * i + 2]))
            for i in range(2):
                evacuate(eng, is_act, f"v{l}{'ab'[i]}", xv[:, l, i, :])

        def evacuate_kve(eng, is_act):
            if by_act("kv") != is_act:
                return
            piece_in(eng, "kv")
            b = pbank("kv")
            put = (lambda d, s: nc.scalar.activation(d, s, ACT.Copy)) if is_act else nc.vector.tensor_copy
            for n in range(2):
                for s in range(2):
                    put(kTe[64 * s:64 * s + 64, n, :], b[64 * n:64 * n + 64, 0:SEQ])
            put(ve.rearrange("p t c -> p (t c)"), b[:, SEQ:2 * SEQ]).then_inc(evac[PIECES["kv"] % 2], 1)

        def odd_piece_out(eng, is_act, m, turns, par):
            k = ODD0 + m
            if (k % 2 == 1) != is_act:
                return
            piece_ready_at = k + 1 + turns * 10
            eng.wait_ge(piece_ready, piece_ready_at)
            b = bank[6 + k % 2]
            put = (lambda d, s: nc.scalar.activation(d, s, ACT.Copy)) if is_act else nc.vector.tensor_copy
            kind = m % 5
            if kind == 0:
                last = put(oq[:, 0:2].rearrange("p g s -> p (g s)"), b[:, :])
            elif kind == 1:
                put(oq[:, 2, :], b[:, 0:SEQ])
                last = put(ok[:, 0, :], b[:, SEQ:2 * SEQ])
            elif kind == 2:
                last = put(ok[:, 1:3].rearrange("p g s -> p (g s)"), b[:, :])
            else:
                last = put(ov[:, par, kind - 3, :], b[:, 0:CG * P])
            last.then_inc(evac[k % 2], 1)

        @block.scalar
        def _(act):
            def copy(dst, src):
                return nc.scalar.activation(dst, src, ACT.Copy)

            act.dma_start(gmem[:, :, :], ln_mem.rearrange("l (p c) -> p l c", c=CH)).then_inc(gmem_in, 16)
            act.dma_start(tab[0:BUCKETS, :], rel_table).then_inc(cst_in, 16)
            act.dma_start(sel33[0:BUCKETS + 1].rearrange("p t c -> p (t c)"), selectors[:, 0:1024]).then_inc(cst_in, 16)
            act.dma_start(uT[0:BUCKETS + 1].rearrange("p t c -> p (t c)"), selectors[:, 1024:2048]).then_inc(cst_in, 16)
            for src, dst in ((ln_mix, gmix), (ln_cross, gcross), (ln_ffn, gffn)):
                act.dma_start(dst[:, :, :], src.rearrange("l (p c) -> p l c", c=CH)).then_inc(par_in, 16)
            for l in range(DEPTH):
                act.dma_start(rw[:, l, :, 0:GROUPS],
                              router_group_w[l].rearrange("(p c) g -> p c g", c=CH)).then_inc(par_in, 16)
                act.dma_start(rw[:, l, :, GROUPS:NR],
                              router_expert_w[l].rearrange("(p c) g e -> p c (g e)", c=CH)).then_inc(par_in, 16)
                act.dma_start(rb[:, l, 0:GROUPS], router_group_b[l].partition_broadcast(P)).then_inc(par_in, 16)
                act.dma_start(rb[:, l, GROUPS:NR],
                              router_expert_b[l].rearrange("g e -> (g e)").partition_broadcast(P)).then_inc(par_in, 16)
            act.dma_start(sink[:, :], attn_sink[0].partition_broadcast(P)).then_inc(par_in, 16)
            act.dma_start(lng, sgu_ln_g[0].partition_broadcast(P)).then_inc(par_in, 16)
            act.dma_start(lnb, sgu_ln_b[0].partition_broadcast(P)).then_inc(par_in, 16)
            act.dma_start(sguw, sgu_w[0].rearrange("g p q -> p g q")).then_inc(par_in, 16)
            act.dma_start(two(sgub), sgu_b[0].rearrange("g p -> (g p)").partition_broadcast(P)).then_inc(par_in, 16)

            def norm(name, middle=lambda: None):
                i = NORM_SEQ[name]
                src = NORMS[name][0]
                norm_source_ready(act, name)
                nc.scalar.activation(rows(0), src[:, 0, :], ACT.Square, accum_out=ssq[:, 0:1]).then_inc(ssq_act, 1)
                if name == "7":
                    return
                act.wait_ge(rstd_set, i + 1)
                nc.scalar.activation(nrm[:, 1, :, 64:P].rearrange("p c q -> p q c"),
                                     src[:, 1, 512:D].rearrange("p (q c) -> p q c", c=CH),
                                     ACT.Copy, scale=rst[:, 1:2]).then_inc(nrm1, 1)
                middle()
                evacuate_norm(act, True, name)

            def exps(a, even):
                act.wait_ge(maxed, a + 1)
                n = a % 2
                if not even and a >= 2:
                    act.wait_ge(pT_ps, a - 1)
                for t in range(2):
                    src = prob[:, n, t, :] if even else bank[n][:, t * 256:(t + 1) * 256]
                    last = nc.scalar.activation(prob[:, n, t, :], src, ACT.Exp, bias=negm[:, n, t:t + 1],
                                                scale=1.0 if even else float(P) ** -0.5,
                                                accum_out=den[:, n, t:t + 1])
                if even:
                    last = nc.scalar.activation(esink[:, n, :], negm[:, n, :], ACT.Exp, bias=sink[:, a:a + 1])
                last.then_inc(exped, 1)

            def pT_out(a):
                act.wait_ge(pT_ps, a + 1)
                if a >= 2:
                    act.wait_ge(pv_ps, a - 1)
                copy(two(probT[:, a % 2]), bank[2 + a % 2][:, :]).then_inc(pT_sb, 1)

            def cross(l):
                for i in range(2):
                    evacuate(act, True, f"xq{l}{'ab'[i]}", two(q4[:, 2 * i:2 * i + 2]))
                for i in range(X_HEADS + 1):
                    if i < X_HEADS:
                        exps(A_X[l] + i, False)
                    if l == 0 and i == 1:
                        evacuate_filler(act, True, "k1b")
                    if i >= 1:
                        pT_out(A_X[l] + i - 1)

            def experts(l):
                act.wait_ge(r_in, 2 * l + 1)
                nc.scalar.activation(eg, gd, ACT.Exp).then_inc(r_exp, 1)
                act.wait_ge(r_in, 2 * l + 2)
                nc.scalar.activation(ex2, m2, ACT.Exp).then_inc(r_exp, 1)
                if l == 0:
                    evacuate_filler(act, True, "v1b")
                for c in range(CH):
                    k = PIECES[f"gather{l}{c}"]
                    if k % 2 == 1:
                        piece_in(act, k)
                        nc.scalar.activation(xg[:, :, c, :], pbank(k).rearrange("p (g s) -> p g s", g=GROUPS),
                                             ACT.Copy, scale=gffn[:, l, c:c + 1]).then_inc(evac[1], 1)
                for name, dst in ((f"gates{l}", None), (f"selT{l}0", two(selT[:, 0:2])), (f"selT{l}1", two(selT[:, 2:4]))):
                    if name[0] == "g":
                        evacuate(act, True, name, two(gslot), src=pbank(name)[:, 0:GROUPS * EPG])
                    else:
                        evacuate(act, True, name, dst)

                def silu_of(x, n, turns):
                    act.wait_ge(gate_ps, x + 1 + turns * EPG)
                    if x >= 2:
                        act.wait_ge(hid_sb, x - 1 + turns * EPG)
                    nc.scalar.activation(silu[:, n, :], bank[0][:, :], ACT.Silu).then_inc(silu_sb, 1)

                def hidT_of(x, turns):
                    act.wait_ge(hT_ps, x + 1 + turns * EPG)
                    copy(two(hidT), bank[2][:, :]).then_inc(hT_sb, 1)

                x0 = l * GROUPS * EPG
                silu_of(x0, 0, 0)

                def group(last, turns):
                    for e in range(EPG):
                        if not (last and e == EPG - 1):
                            silu_of(x0 + e + 1, (e + 1) % 2, turns)
                        hidT_of(x0 + e, turns)

                with act.Fori(0, GROUPS - 1) as g:
                    group(False, g)
                group(True, GROUPS - 1)
                second_pass(l)

            def second_pass(l):
                s = second[l]
                act.wait_ge(ovf_set, l + 1)
                flag = act.value_load(ovf[0:1, l, 0:1], min_val=0, max_val=1)
                with act.If(flag > 0):
                    with act.Fori(0, EPG) as e:
                        act.wait_ge(s["gate_ps"], e + 1)
                        nc.scalar.activation(silu[:, 0, :], bank[0][:, :], ACT.Silu).then_inc(s["silu"], 1)
                        act.wait_ge(s["hT_ps"], e + 1)
                        copy(two(hidT), bank[2][:, :]).then_inc(s["hT_sb"], 1)

            norm("m")
            norm("1", lambda: evacuate_kv(act, True, 0))
            for t in range(TILES):
                evacuate(act, True, f"va{t}", va[:, t, :], func=ACT.Gelu_apprx_tanh)
            for i in range(2):
                evacuate(act, True, f"q{i}", two(q4[:, 2 * i:2 * i + 2]))
            evacuate_kve(act, True)
            for i in range(B_HEADS + 2):
                if i < B_HEADS:
                    exps(i, True)
                if FILL[i]:
                    evacuate_filler(act, True, FILL[i])
                if 1 <= i <= B_HEADS:
                    pT_out(i - 1)
            norm("2")
            cross(0)
            norm("3")
            experts(0)
            norm("4")

            def o_proj_out(m, rounds, par):
                odd_piece_out(act, True, m, rounds, par)

            def o_exps(i, n, turns=0):
                act.wait_ge(o_maxed, i + 1 + turns * 2)
                for t in range(2):
                    last = nc.scalar.activation(op[:, :, t, :], op[:, :, t, :], ACT.Exp, bias=negm[:, n, t:t + 1],
                                                accum_out=den[:, n, t:t + 1])
                last.then_inc(o_exped, 1)

            def o_pT_out(i, turns=0):
                for g in range(CG):
                    act.wait_ge(o_pT_ps, CG * i + g + 1 + turns * 2 * CG)
                    copy(opT[:, g].rearrange("p b q -> p (b q)"),
                         bank[2 + (CG * i + g) % 2][:, :]).then_inc(o_pT_sb, 1)

            def o_head(i, nxt, turns=0):
                o_exps(i, i % 2, turns)
                for m in range(5):
                    if m == 3:
                        o_pT_out(i, turns)
                    if nxt:
                        o_proj_out(5 * (i + 1) + m, turns, (i + 1) % 2)

            for m in range(5):
                o_proj_out(m, 0, 0)
            with act.Fori(0, C_HEADS // 2 - 1) as j:
                for i in range(2):
                    o_head(i, True, j)
            o_head(C_HEADS - 2, True)
            o_head(C_HEADS - 1, False)
            norm("5")
            cross(1)
            norm("6")
            experts(1)
            norm("7")

        @block.gpsimd
        def _(pool):
            pool.memset(tab[BUCKETS:BUCKETS + 1, :], MASKED).then_inc(tab_set, 1)
            pool.wait_ge(vec_sb, 1)
            v = vec[0:B_HEADS].rearrange("p j s -> p (j s)").rearrange("p (m x) -> p m x", x=SPAN)
            for m in range(1 + CG):
                pool.dma_start(biasd[m].rearrange("(h x) -> h x", h=B_HEADS)[:, 0:SKEW * SPAN].rearrange("h (r x) -> h r x", x=SPAN),
                               v[:, m, :].unsqueeze(1).to_broadcast([B_HEADS, SKEW, SPAN])).then_inc(bias_out, 16)
            pool.wait_ge(bias_out, 16 * (1 + CG))

            for a in range(P // SKEW):
                pool.dma_start(tbias[SKEW * a:SKEW * (a + 1)], skewed(biasd[0].rearrange("(h x) -> h x", h=B_HEADS), a)).then_inc(tbias_in, 16)

            def second_pass(l):
                s = second[l]
                pool.wait_ge(ovf_set, l + 1)
                flag = pool.value_load(ovf[0:1, l, 0:1], min_val=0, max_val=1)
                g = pool.value_load(ovf[0:1, l, 1:2], min_val=0, max_val=GROUPS - 1)

                def w(src, e):
                    return src[l, g, e].rearrange("(p c) n -> p (c n)", p=P)

                with pool.If(flag > 0):
                    pool.wait_ge(resid, (R_MOE0, R_MOE1)[l] + 4)
                    for e in range(EPG):
                        if e:
                            pool.wait_ge(s["y_ps"], e)
                        pool.dma_start(wa, w(expert_w_gate, e)).then_inc(s["gate_in"], 16)
                        pool.dma_start(wb, w(expert_w_up, e)).then_inc(s["up_in"], 16)
                        pool.wait_ge(s["gate_ps"], e + 1)
                        pool.dma_start(wa, w(expert_w_down, e)).then_inc(s["down_in"], 16)

            second_pass(0)

            second_pass(1)
            pool.wait_ge(moe_done, 2)
            pool.dma_start(lnf, ln_final.partition_broadcast(P)).then_inc(lnf_in, 16)

        @block.tensor
        def _(pe):
            free = [0]

            def slots_read(n=1):
                free[0] += n

            def giving_back(ins):
                if free[0]:
                    ins.then_inc(ring_used, free[0])
                    free[0] = 0
                return ins

            def mm(dst, lhsT, rhs, start, stop):
                return giving_back(nc.tensor.matmul(dst, lhsT, rhs, start=start, stop=stop))

            def flip(dst, src):
                return giving_back(nc.tensor.transpose(dst, src, ident))

            def columns(pb, w, src, half):
                for i in range(2):
                    for c in range(CH):
                        last = mm(pb[:, i * SEQ:(i + 1) * SEQ], w(c, 2 * half + i), src[:, c, :], c == 0, c == CH - 1)
                return last

            def full(n):
                return slot(n).rearrange("p (c n) -> p c n", c=CH)

            def norm(name):
                i = NORM_SEQ[name]
                pe.wait_ge(nrm0, i + 1)
                pe.wait_ge(nrm1a, i + 1)
                pe.wait_ge(nrm1, i + 1)
                if name == "m":
                    pe.wait_ge(id_in, 16)
                for j in range(4):
                    k = f"n{name}{j}"
                    piece_free(pe, k)
                    for c in (2 * j, 2 * j + 1):
                        for t in range(TILES):
                            at = (c % 2) * SEQ + t * P
                            last = flip(pbank(k)[:, at:at + P], nrm[:, t, c, :])
                    last.then_inc(piece_ready, 1)

            def normed(name):
                for j in (2, 3):
                    piece_out(pe, f"n{name}{j}")

            def col_piece(name, n, w, src, half, free=False):
                piece_free(pe, name)
                last = columns(pbank(name), w, src, half)
                last.then_inc(piece_ready, 1)
                return last

            def plain(n):
                return lambda c, b: full(n)[:, c, b * P:(b + 1) * P]

            def keys(l, half):
                n = (W_K0, W_K1)[l]
                arrived(pe, n)
                src = (nT, mT1)[l]
                name = f"k{l}{'ab'[half]}"
                piece_free(pe, name)
                last = columns(pbank(name), plain(n), src, half)
                last.then_inc(piece_ready, 1)

            def values(l, t):
                n = (W_V0, W_V1)[l]
                arrived(pe, n)
                src = (nT, mT1)[l]
                name = f"v{l}{'ab'[t]}"
                piece_free(pe, name)
                for c in range(CH):
                    last = mm(pbank(name)[:, :], src[:, c, t * P:(t + 1) * P], full(n)[:, c, :], c == 0, c == CH - 1)
                last.then_inc(piece_ready, 1)

            def transposes(a):
                pe.wait_ge(probs, a + 1)
                if a >= 2:
                    pe.wait_ge(pT_sb, a - 1)
                b = bank[2 + a % 2]
                for kb in range(2):
                    for t in range(2):
                        last = flip(b[:, kb * 256 + t * P:kb * 256 + (t + 1) * P],
                                                   prob[:, a % 2, t, kb * P:(kb + 1) * P])
                last.then_inc(pT_ps, 1)

            def outputs(a, v):
                pe.wait_ge(pT_sb, a + 1)
                if a >= 2:
                    pe.wait_ge(pv_sb, a - 1)
                for kb in range(2):
                    last = mm(bank[4 + a % 2][:, 0:SEQ], v(kb), probT[:, a % 2, kb, :], kb == 0, kb == 1)
                last.then_inc(pv_ps, 1)

            def scores_of(a, q, k):
                if a >= 2:
                    pe.wait_ge(exped, a - 1)
                for t in range(TILES):
                    last = mm(bank[a % 2][:, t * 256:(t + 1) * 256], q(t), k, True, True)
                last.then_inc(scores, 1)

            def project(src, blocks, weights, first=True, final=True):
                for t in range(TILES):
                    for f in range(2):
                        for n, js in weights:
                            if t == 0 and f == 0:
                                arrived(pe, n)
                            w = slot(n).rearrange("p (j n) -> p j n", j=4)
                            for jj, j in enumerate(js):
                                last = mm(bank[2 * t + f][:, :], src[:, j, t * P:(t + 1) * P],
                                          w[:, jj, f * 512:(f + 1) * 512], j == 0, j == blocks - 1)
                        last.then_inc(proj, 1)
                slots_read(len(weights))

            norm("m")
            normed("m")
            keys(0, 0)
            keys(0, 1)
            values(0, 0)
            values(0, 1)
            slots_read(2)

            pe.wait_ge(cst_in, 16 * 3)
            pe.wait_ge(tab_set, 1)
            for m in range(1 + CG):
                e = (two(sel33) if m < 2 else two(uT))[0:BUCKETS + 1, (m % 2) * SPAN:(m % 2 + 1) * SPAN]
                last = mm(bank[m][0:B_HEADS, :], tab[:, :], e, True, True)
            last.then_inc(vec_ps, 1)

            norm("1")
            normed("1")
            for t in range(TILES):
                if t == 0:
                    arrived(pe, W_VA)
                name = f"va{t}"
                piece_free(pe, name)
                for c in range(CH):
                    last = mm(pbank(name)[:, :], nT[:, c, t * P:(t + 1) * P], full(W_VA)[:, c, :], c == 0, c == CH - 1)
                last.then_inc(piece_ready, 1)
            slots_read()
            arrived(pe, W_Q)

            for i in range(2):
                col_piece(f"q{i}", W_Q, plain(W_Q), nT, i)
            arrived(pe, W_KV)
            piece_free(pe, "kv")
            wkv = slot(W_KV)[:, 0:CH * 256].rearrange("p (c n) -> p c n", c=CH)
            for c in range(CH):
                mm(pbank("kv")[:, 0:SEQ], wkv[:, c, 0:P], nT[:, c, :], c == 0, c == CH - 1)
            for t in range(TILES):
                for c in range(CH):
                    last = mm(pbank("kv")[:, SEQ + t * P:SEQ + (t + 1) * P], nT[:, c, t * P:(t + 1) * P],
                              wkv[:, c, P:2 * P], c == 0, c == CH - 1)
            last.then_inc(piece_ready, 1)
            slots_read(2)
            piece_out(pe, "kv")

            def fill(name):
                if name == "wsT":
                    piece_free(pe, name)
                    for g in range(A_GROUPS):
                        last = flip(pbank(name)[:, g * P:(g + 1) * P], sguw[:, g, :])
                    last.then_inc(piece_ready, 1)
                elif name in ("u0", "u1"):
                    arrived(pe, W_U)
                    col_piece(name, W_U, plain(W_U), nT, int(name[1]))
                elif name in ("mix0", "mix1"):
                    pe.wait_ge(vn_set, TILES)
                    piece_out(pe, "wsT")
                    piece_free(pe, name)
                    for gg in range(2):
                        g = 2 * int(name[3]) + gg
                        for t in range(TILES):
                            at = gg * SEQ + t * P
                            last = mm(pbank(name)[:, at:at + P], va[:, t, g * P:(g + 1) * P], wsT[:, g, :], True, True)
                    last.then_inc(piece_ready, 1)
                elif name in ("k1a", "k1b"):
                    keys(1, "ab".index(name[2]))
                elif name in ("v1a", "v1b"):
                    values(1, "ab".index(name[2]))

            for i in range(B_HEADS + 2):
                if i < B_HEADS:
                    b, s = divmod(i, 2)
                    if i == 0:
                        piece_out(pe, "q0")
                        piece_out(pe, "q1")
                    scores_of(i, lambda t: q4[64 * s:64 * s + 64, b, t * P:(t + 1) * P], kTe[64 * s:64 * s + 64, i // 4, :])
                if FILL[i]:
                    fill(FILL[i])
                if FILL[i] == "u1":
                    slots_read()
                if 1 <= i <= B_HEADS:
                    transposes(i - 1)
                if i >= 2:
                    outputs(i - 2, lambda kb: ve[:, kb, :])
            pe.wait_ge(ya_set, 2)
            pe.wait_ge(pv_sb, B_HEADS)
            project(yT, 8, [(W_OA, range(4)), (W_OB, range(4, 8))])
            keys(1, 0)

            def cross(l, name):
                norm(name)
                normed(name)
                arrived(pe, W_XQ[l])
                for i in range(2):
                    col_piece(f"xq{l}{'ab'[i]}", W_XQ[l], plain(W_XQ[l]), nT, i)
                slots_read()
                for i in range(X_HEADS + 2):
                    if i < X_HEADS:
                        if i % 2 == 0:
                            piece_out(pe, f"xq{l}{'ab'[i // 2]}")
                        scores_of(A_X[l] + i, lambda t: q4[:, i, t * P:(t + 1) * P], xkT[:, l, i, :])
                    if l == 0 and i == 1:
                        keys(1, 1)
                        slots_read()
                    if 1 <= i <= X_HEADS:
                        transposes(A_X[l] + i - 1)
                    if i >= 2:
                        hd = i - 2
                        outputs(A_X[l] + hd, lambda kb: xv[:, l, kb, hd * P:(hd + 1) * P])
                pe.wait_ge(pv_sb, A_X[l] + X_HEADS)
                project(yT, 4, [(W_XO[l], range(4))])
                if l == 0:
                    values(1, 0)

            def experts(l, name):
                norm(name)
                normed(name)
                k = f"router{l}"
                piece_free(pe, k)
                for t in range(TILES):
                    for c in range(CH):
                        last = mm(pbank(k)[:, t * NR:(t + 1) * NR], nT[:, c, t * P:(t + 1) * P], rw[:, l, c, :],
                                  c == 0, c == CH - 1)
                last.then_inc(piece_ready, 1)
                if l == 0:
                    values(1, 1)
                    slots_read()
                k = f"pos{l}"
                piece_free(pe, k)
                pe.wait_ge(oh_set, l + 1)
                b = pbank(k)
                mm(b[:, 0:4], earlier, oh[:, 0, :], True, True)
                mm(b[:, 4:8], ones, oh[:, 0, :], True, False)
                mm(b[:, 4:8], earlier, oh[:, 1, :], False, True)
                mm(b[:, 8:12], ones, oh[:, 0, :], True, False)
                mm(b[:, 8:12], ones, oh[:, 1, :], False, True).then_inc(piece_ready, 1)
                pe.wait_ge(sel_set, TILES * (l + 1))
                for c in range(CH):
                    k = f"gather{l}{c}"
                    piece_free(pe, k)
                    for t in range(TILES):
                        last = mm(pbank(k)[:, :], nrm[:, t, c, :], two(sel[:, t]), t == 0, t == 1)
                    last.then_inc(piece_ready, 1)
                k = f"gates{l}"
                piece_free(pe, k)
                for g in range(GROUPS):
                    for t in range(TILES):
                        last = mm(pbank(k)[:, g * EPG:(g + 1) * EPG], sel[:, t, g, :], gate[:, t, :], t == 0, t == 1)
                last.then_inc(piece_ready, 1)
                for i in range(2):
                    k = f"selT{l}{i}"
                    piece_free(pe, k)
                    for gg in range(2):
                        for t in range(TILES):
                            at = gg * SEQ + t * P
                            last = flip(pbank(k)[:, at:at + P], sel[:, t, 2 * i + gg, :])
                    last.then_inc(piece_ready, 1)

                x0 = l * GROUPS * EPG
                base = W_MOE[l]

                def products(b, n, later, ready):
                    arrived(pe, n, later)
                    for c in range(CH):
                        last = mm(b[:, :], xcur[:, c, :], full(n)[:, c, :], c == 0, c == CH - 1)
                    last.then_inc(ready, 1)
                    slots_read()

                def gate_up(x, n, turns, later, between=lambda: None):
                    if x > x0:
                        pe.wait_ge(silu_sb, x + turns * EPG)
                    products(bank[0], n, later, gate_ps)
                    between()
                    if x > x0:
                        pe.wait_ge(hid_sb, x + turns * EPG)
                    products(bank[1], n + 1, later, up_ps)

                def turn(x, turns):
                    pe.wait_ge(hid_sb, x + 1 + turns * EPG)
                    for c in range(FC):
                        last = flip(bank[2][:, c * P:(c + 1) * P], hid[:, c, :])
                    last.then_inc(hT_ps, 1)

                def down(x, e, n, turns, later):
                    arrived(pe, n, later)
                    pe.wait_ge(hT_sb, x + 1 + turns * EPG)
                    w = slot(n).rearrange("p (c n) -> p c n", c=FC)
                    for c in range(FC):
                        for f in range(2):
                            last = mm(bank[3 + f][:, :], hidT[:, c, :], w[:, c, f * 512:(f + 1) * 512],
                                      e == 0 and c == 0, e == EPG - 1 and c == FC - 1)
                    if e == EPG - 1:
                        last.then_inc(y_ps, 1)
                    slots_read()

                pe.wait_ge(xcur_set, l * GROUPS + 1)
                gate_up(x0, base, 0, 0)

                def group(last, turns):
                    later = turns * 32
                    n = base + 2
                    for e in range(EPG):
                        x = x0 + e
                        if last and e == EPG - 1:
                            turn(x, turns)
                        else:
                            if e == EPG - 1:
                                pe.wait_ge(xcur_set, l * GROUPS + 2 + turns)
                            gate_up(x + 1, n, turns, later, lambda: turn(x, turns))
                            n += 2
                        if e == 0:
                            pe.wait_ge(y_free, l * (GROUPS + 1) + 1 + turns)
                        down(x, e, n, turns, later)
                        n += 1

                with pe.Fori(0, GROUPS - 1) as g:
                    group(False, g)
                group(True, GROUPS - 1)

                pe.wait_ge(y_free, (l + 1) * (GROUPS + 1))
                for t in range(TILES):
                    for f in range(2):
                        b = scatter_bank(2 * t + f)
                        for g in range(GROUPS):
                            last = mm(b[:, :], selT[:, g, t * P:(t + 1) * P], ysb[:, g, f * 512:(f + 1) * 512],
                                      g == 0, g == GROUPS - 1)
                        last.then_inc(proj, 1)
                second_pass(l)

            def second_pass(l):
                s = second[l]
                pe.wait_ge(ovf_set, l + 1)
                flag = pe.value_load(ovf[0:1, l, 0:1], min_val=0, max_val=1)
                with pe.If(flag > 0):
                    pe.wait_ge(s["sel"], TILES)
                    pe.wait_ge(resid, (R_MOE0, R_MOE1)[l] + 4)
                    for t in range(TILES):
                        last = flip(bank[0][:, t * P:(t + 1) * P], sel2[:, t, :])
                    last.then_inc(s["parts"], 1)
                    for t in range(TILES):
                        last = mm(bank[1][:, 0:EPG], sel2[:, t, :], gate[:, t, :], t == 0, t == 1)
                    last.then_inc(s["parts"], 1)
                    for c in range(CH):
                        for t in range(TILES):
                            last = mm(bank[2 + c // 4][:, (c % 4) * P:(c % 4 + 1) * P], nrm[:, t, c, :], sel2[:, t, :],
                                      t == 0, t == 1)
                    last.then_inc(s["parts"], 1)
                    pe.wait_ge(s["tokens"], 1)
                    with pe.Fori(0, EPG) as e:
                        for b, w, came, ready in ((0, wa, "gate_in", "gate_ps"), (1, wb, "up_in", "up_ps")):
                            pe.wait_ge(s[came], e * 16 + 16)
                            v = w.rearrange("p (c n) -> p c n", c=CH)
                            for c in range(CH):
                                last = mm(bank[b][:, :], xcur[:, c, :], v[:, c, :], c == 0, c == CH - 1)
                            last.then_inc(s[ready], 1)
                        pe.wait_ge(s["hid"], e + 1)
                        for c in range(FC):
                            last = flip(bank[2][:, c * P:(c + 1) * P], hid[:, c, :])
                        last.then_inc(s["hT_ps"], 1)
                        pe.wait_ge(s["hT_sb"], e + 1)
                        pe.wait_ge(s["down_in"], e * 16 + 16)
                        pe.wait_ge(s["y_sb"], e + 1)
                        v = wa.rearrange("p (c n) -> p c n", c=FC)
                        for c in range(FC):
                            for f in range(2):
                                last = mm(bank[3 + f][:, :], hidT[:, c, :], v[:, c, f * 512:(f + 1) * 512],
                                          c == 0, c == FC - 1)
                        last.then_inc(s["y_ps"], 1)
                    pe.wait_ge(s["y_sb"], EPG + 1)
                    for t in range(TILES):
                        for f in range(2):
                            mm(scatter_bank(2 * t + f)[:, :], selT[:, 0, t * P:(t + 1) * P],
                               acc2[:, f * 512:(f + 1) * 512], True, True).then_inc(s["proj"], 1)

            cross(0, "2")
            experts(0, "3")

            norm("4")
            normed("4")

            def head_piece(m, par, turns):
                k = ODD0 + m
                piece_free(pe, k, turns * 5)
                b = bank[6 + k % 2]
                hd, kind = divmod(m, 5)
                n = W_ODD + 3 * hd
                later = turns * 48

                def w(which):
                    return slot(n + which)[:, 0:CH * CG * P].rearrange("p (c n) -> p c n", c=CH)

                if kind < 3:
                    if kind < 2:
                        arrived(pe, n + kind, later)
                    for i in range(2):
                        which, g = divmod(2 * kind + i, CG)
                        for c in range(CH):
                            last = mm(b[:, i * SEQ:(i + 1) * SEQ], w(which)[:, c, g * P:(g + 1) * P], nT[:, c, :],
                                      c == 0, c == CH - 1)
                else:
                    if kind == 3:
                        arrived(pe, n + 2, later)
                    t = kind - 3
                    for c in range(CH):
                        last = mm(b[:, 0:CG * P], nT[:, c, t * P:(t + 1) * P], w(2)[:, c, :], c == 0, c == CH - 1)
                last.then_inc(piece_ready, 1)
                if kind in (1, 2, 4):
                    slots_read()

            S_BANK = (0, 1, 5)

            def head(i, nxt, turns=0):
                piece_out(pe, ODD0 + 5 * i + 1, turns * 5)
                piece_out(pe, ODD0 + 5 * i + 2, turns * 5)
                for g in range(CG):
                    for t in range(TILES):
                        last = mm(bank[S_BANK[g]][:, t * 256:(t + 1) * 256], oq[:, g, t * P:(t + 1) * P], ok[:, g, :],
                                  True, True)
                    last.then_inc(o_scores, 1)
                if nxt:
                    for m in range(3):
                        head_piece(5 * (i + 1) + m, (i + 1) % 2, turns)
                pe.wait_ge(o_probs, i + 1 + turns * 2)
                for g in range(CG):
                    x = CG * i + g
                    if x >= 2:
                        pe.wait_ge(o_pT_sb, x - 1 + turns * 2 * CG)
                    b = bank[2 + x % 2]
                    for kb in range(2):
                        for t in range(2):
                            last = flip(b[:, kb * 256 + t * P:kb * 256 + (t + 1) * P],
                                                       op[:, g, t, kb * P:(kb + 1) * P])
                    last.then_inc(o_pT_ps, 1)
                if nxt:
                    head_piece(5 * (i + 1) + 3, (i + 1) % 2, turns)
                pe.wait_ge(o_pT_sb, CG * (i + 1) + turns * 2 * CG)
                for g in range(CG):
                    for kb in range(2):
                        last = mm(bank[4][:, 0:SEQ], ov[:, i % 2, kb, g * P:(g + 1) * P], opT[:, g, kb, :],
                                  g == 0 and kb == 0, g == CG - 1 and kb == 1)
                last.then_inc(o_pv_ps, 1)
                if nxt:
                    head_piece(5 * (i + 1) + 4, (i + 1) % 2, turns)
                    piece_out(pe, ODD0 + 5 * (i + 1) + 2, turns * 5)

            for m in range(5):
                head_piece(m, 0, 0)
            with pe.Fori(0, C_HEADS // 2 - 1) as j:
                for i in range(2):
                    head(i, True, j)
            head(C_HEADS - 2, True)
            head(C_HEADS - 1, False)
            pe.wait_ge(o_pv_sb, C_HEADS)
            project(oyT, 8, [(W_OO, range(4)), (W_OO + 1, range(4, 8))])
            cross(1, "5")
            experts(1, "6")

        @block.vector
        def _(dve):
            steps = [0]

            def step(ins):
                steps[0] += 1
                ins.then_inc(dve_step, 1)
                dve.wait_ge(dve_step, steps[0])

            v = nc.vector

            def rsqrt(tiles):
                cols = [slice(t, t + 1) for t in tiles]

                def each(op):
                    for c in cols:
                        last = op(c)
                    return last

                step(each(lambda c: v.tensor_scalar(seed[:, c], var[:, c].bitcast(I32), 1, None,
                                                    ALU.logical_shift_right)))
                step(each(lambda c: v.tensor_scalar(seed[:, c], seed[:, c], -1.0, MAGIC, ALU.mult, ALU.add)))
                for three in (3.0, 12.0, 768.0):
                    def y(c):
                        return seed[:, c].bitcast(F32) if three == 3.0 else rst[:, c]

                    step(each(lambda c: v.scalar_tensor_tensor(out=tmp[:, c], in0=y(c), scalar=y(c), in1=var[:, c],
                                                               op0=ALU.mult, op1=ALU.mult)))
                    step(each(lambda c: v.scalar_tensor_tensor(out=rst[:, c], in0=tmp[:, c], scalar=-three, in1=y(c),
                                                               op0=ALU.add, op1=ALU.mult)))
                return each(lambda c: v.tensor_scalar(rst[:, c], rst[:, c], RSQRT_FACTOR, None, ALU.mult))

            def add(at, i):
                t, f = divmod(i, 2)
                dve.wait_ge(proj, at + i + 1)
                b = scatter_bank(i) if at in (R_MOE0, R_MOE1) else bank[i]
                r = h[:, t, f * 512:(f + 1) * 512]
                v.tensor_tensor(r, b[:, :], r, ALU.add).then_inc(resid, 1)

            def norm(name, middle=lambda: None):
                i = NORM_SEQ[name]
                src = NORMS[name][0]
                at = AFTER.get(name)
                if at is None:
                    norm_source_ready(dve, name)
                if i:
                    dve.wait_ge(nrm1, i)

                def squares(f):
                    part = src[:, 1, f * 512:(f + 1) * 512]
                    step(v.tensor_tensor_reduce(rows(1)[:, f * 512:(f + 1) * 512], part, part, 1.0, 0.0, ALU.mult,
                                                ALU.add, ssq[:, 1 + f:2 + f]))

                def variance(t):
                    step(v.tensor_scalar(var[:, t:t + 1], ssq[:, t:t + 1], 1.0 / D, EPS, ALU.mult, ALU.add))

                def scale0():
                    if name == "7":
                        dve.wait_ge(lnf_in, 16)
                        v.scalar_tensor_tensor(out=rows(0), in0=src[:, 0, :], scalar=rst[:, 0:1], in1=lnf,
                                               op0=ALU.mult, op1=ALU.mult).then_inc(fin_set, 1)
                    else:
                        v.tensor_scalar(nrm[:, 0].rearrange("p c q -> p q c"),
                                        src[:, 0, :].rearrange("p (q c) -> p q c", c=CH),
                                        rst[:, 0:1], None, ALU.mult).then_inc(nrm0, 1)

                if at is None:
                    squares(0)
                    squares(1)
                    step(v.tensor_tensor(ssq[:, 1:2], ssq[:, 1:2], ssq[:, 2:3], ALU.add))
                    dve.wait_ge(ssq_act, i + 1)
                    step(v.tensor_scalar(var[:, :], ssq[:, 0:2], 1.0 / D, EPS, ALU.mult, ALU.add))
                    rsqrt([0, 1]).then_inc(rstd_set, 1)
                    dve.wait_ge(rstd_set, i + 1)
                    scale0()
                else:
                    add(at, 0)
                    add(at, 1)
                    dve.wait_ge(ssq_act, i + 1)
                    variance(0)
                    step(rsqrt([0]))
                    scale0()
                    for f in range(2):
                        add(at, 2 + f)
                        dve.wait_ge(resid, at + 3 + f)
                        squares(f)
                    step(v.tensor_tensor(ssq[:, 1:2], ssq[:, 1:2], ssq[:, 2:3], ALU.add))
                    variance(1)
                    rsqrt([1]).then_inc(rstd_set, 1)
                    dve.wait_ge(rstd_set, i + 1)
                if name == "7":
                    v.scalar_tensor_tensor(out=rows(1), in0=src[:, 1, :], scalar=rst[:, 1:2], in1=lnf, op0=ALU.mult,
                                           op1=ALU.mult).then_inc(fin_set, 1)
                    return
                v.tensor_scalar(nrm[:, 1, :, 0:64].rearrange("p c q -> p q c"),
                                src[:, 1, 0:512].rearrange("p (q c) -> p q c", c=CH),
                                rst[:, 1:2], None, ALU.mult).then_inc(nrm1a, 1)
                middle()
                evacuate_norm(dve, False, name)

            def maxima(a, even):
                n = a % 2
                dve.wait_ge(scores, a + 1)
                if even:
                    if a == 0:
                        dve.wait_ge(tbias_in, 16 * (P // SKEW))
                    if a >= 2:
                        dve.wait_ge(pT_ps, a - 1)
                    for t in range(2):
                        last = v.scalar_tensor_tensor(out=prob[:, n, t, :], in0=bank[n][:, t * 256:(t + 1) * 256],
                                                      scalar=float(B_DIM) ** -0.5,
                                                      in1=tbias[:, a, P - t * P:P - t * P + 256],
                                                      op0=ALU.mult, op1=ALU.add)
                    step(last)
                    step(v.tensor_reduce(mx[:, n, :], prob[:, n], AX.X, ALU.max))
                    v.tensor_scalar(negm[:, n, :], mx[:, n, :], sink[:, a:a + 1], -1.0, ALU.max,
                                    ALU.mult).then_inc(maxed, 1)
                else:
                    step(v.tensor_reduce(mx[:, n, :], bank[n].rearrange("p (t k) -> p t k", t=2), AX.X, ALU.max))
                    v.tensor_scalar(negm[:, n, :], mx[:, n, :], -float(P) ** -0.5, None, ALU.mult).then_inc(maxed, 1)

            def normalise(a, even):
                n = a % 2
                dve.wait_ge(exped, a + 1)
                if even:
                    step(v.tensor_tensor(den[:, n, :], den[:, n, :], esink[:, n, :], ALU.add))
                step(v.reciprocal(rden[:, n, :], den[:, n, :]))
                for t in range(2):
                    last = v.tensor_scalar(prob[:, n, t, :], prob[:, n, t, :], rden[:, n, t:t + 1], None, ALU.mult)
                last.then_inc(probs, 1)

            def head_out(a, even, hd):
                dve.wait_ge(pv_ps, a + 1)
                b = bank[4 + a % 2]
                if even:
                    j, s = divmod(hd, 2)
                    kv = hd // 4
                    dst, src = yT[64 * s:64 * s + 64, 4 + j, :], b[64 * kv:64 * kv + 64, 0:SEQ]
                else:
                    dst, src = yT[:, hd, :], b[:, 0:SEQ]
                v.tensor_copy(dst, src).then_inc(pv_sb, 1)

            def layer_norm_values():
                for t in range(TILES):
                    piece_out(dve, f"va{t}")
                    step(v.bn_stats(stats[:, t, :], va[:, t, :]))
                    step(v.bn_aggr(aggr[:, t, :], stats[:, t, :]))
                dve.wait_ge(nrm1, NORM_SEQ["1"] + 1)
                step(v.tensor_scalar(var[:, :], aggr[:, :, 1], EPS, None, ALU.add))
                step(rsqrt([0, 1]))
                for t in range(TILES):
                    step(v.tensor_scalar(va[:, t, :], va[:, t, :], aggr[:, t, 0:1], rst[:, t:t + 1], ALU.subtract, ALU.mult))
                    step(v.tensor_tensor(va[:, t, :], va[:, t, :], lng, ALU.mult))
                    v.tensor_tensor(va[:, t, :], va[:, t, :], lnb, ALU.add).then_inc(vn_set, 1)

            def gated(name):
                i = int(name[3])
                k = PIECES[name]
                piece_in(dve, name)
                y = yT[:, 2 * i:2 * i + 2].rearrange("p g (t q) -> p g t q", t=TILES)
                b = sgub[:, 2 * i:2 * i + 2].unsqueeze(2).to_broadcast([P, 2, TILES, P])
                v.tensor_tensor(y, pbank(name).rearrange("p (g t q) -> p g t q", g=2, t=TILES), b,
                                ALU.add).then_inc(evac[k % 2], 1)
                piece_out(dve, name)
                piece_out(dve, f"u{i}")
                yy = two(yT[:, 2 * i:2 * i + 2])
                v.tensor_tensor(yy, yy, two(uT[:, 2 * i:2 * i + 2]), ALU.mult).then_inc(ya_set, 1)

            norm("m")
            def first_pieces():
                evacuate_kv(dve, False, 0)
                dve.wait_ge(vec_ps, 1)
                for m in range(1 + CG):
                    last = v.tensor_copy(two(vec[0:B_HEADS])[:, m * SPAN:(m + 1) * SPAN], bank[m][0:B_HEADS, :])
                last.then_inc(vec_sb, 1)

            norm("1", first_pieces)
            for i in range(2):
                evacuate(dve, False, f"q{i}", two(q4[:, 2 * i:2 * i + 2]))
            evacuate_kve(dve, False)
            layer_norm_values()
            dve.wait_ge(bias_out, 16 * (1 + CG))
            for i in range(B_HEADS + 2):
                if i < B_HEADS:
                    maxima(i, True)
                if FILL[i] in ("mix0", "mix1"):
                    gated(FILL[i])
                elif FILL[i]:
                    evacuate_filler(dve, False, FILL[i])
                if 1 <= i <= B_HEADS:
                    normalise(i - 1, True)
                if i >= 2:
                    head_out(i - 2, True, i - 2)
            norm("2")

            def cross(l):
                for i in range(2):
                    evacuate(dve, False, f"xq{l}{'ab'[i]}", two(q4[:, 2 * i:2 * i + 2]))
                for i in range(X_HEADS + 2):
                    if i < X_HEADS:
                        maxima(A_X[l] + i, False)
                    if l == 0 and i == 1:
                        evacuate_filler(dve, False, "k1b")
                    if 1 <= i <= X_HEADS:
                        normalise(A_X[l] + i - 1, False)
                    if i >= 2:
                        head_out(A_X[l] + i - 2, False, i - 2)

            def per_token(x, n):
                return x.unsqueeze(2).to_broadcast([P, TILES, n])

            def first_hit(dst, hits):
                step(v.tensor_tensor(dst, hits, first4, ALU.mult))
                step(v.tensor_reduce(mw, dst, AX.X, ALU.max))
                step(v.tensor_tensor(dst, dst, per_token(mw, 4), ALU.is_equal))

            def route(l):
                k = f"router{l}"
                piece_in(dve, k)
                v.tensor_tensor(lg, pbank(k)[:, 0:TILES * NR].rearrange("p (t n) -> p t n", t=TILES),
                                rb[:, l].unsqueeze(1).to_broadcast([P, TILES, NR]), ALU.add).then_inc(evac[PIECES[k] % 2], 1)
                piece_out(dve, k)
                glog, elog = lg[:, :, 0:GROUPS], lg[:, :, GROUPS:NR]
                step(v.tensor_reduce(gm, glog, AX.X, ALU.max))
                step(v.tensor_tensor(gd, glog, per_token(gm, 4), ALU.subtract))
                v.tensor_scalar(eq, gd, 0.0, None, ALU.is_equal).then_inc(r_in, 1)
                dve.wait_ge(r_in, 2 * l + 1)
                first_hit(oh, eq)
                v.tensor_copy(gate2, oh).then_inc(oh_set, 1)
                dve.wait_ge(oh_set, l + 1)
                for t in range(TILES):
                    last = v.tensor_tensor(prod[:, t], elog[:, t].rearrange("p (g e) -> p g e", g=GROUPS),
                                           oh[:, t].unsqueeze(2).to_broadcast([P, GROUPS, EPG]), ALU.mult)
                step(last)
                step(v.tensor_reduce(esel, prod.rearrange("p t g e -> p t e g"), AX.X, ALU.add))
                step(v.tensor_reduce(m1, esel, AX.X, ALU.max))
                step(v.tensor_tensor(esel, esel, per_token(m1, 4), ALU.subtract))
                step(v.tensor_scalar(eq, esel, 0.0, None, ALU.is_equal))
                first_hit(oh1, eq)
                step(v.scalar_tensor_tensor(out=e2, in0=oh1, scalar=MASKED, in1=esel, op0=ALU.mult, op1=ALU.add))
                v.tensor_reduce(m2, e2, AX.X, ALU.max).then_inc(r_in, 1)
                dve.wait_ge(r_in, 2 * l + 2)
                step(v.tensor_tensor(eq, e2, per_token(m2, 4), ALU.is_equal))
                first_hit(oh2, eq)
                dve.wait_ge(r_exp, 2 * l + 2)
                step(v.tensor_reduce(gsum, eg, AX.X, ALU.add))
                step(v.reciprocal(ggate, gsum))
                step(v.tensor_scalar(w1, ex2, 1.0, None, ALU.add))
                step(v.reciprocal(w1, w1))
                step(v.tensor_tensor(w1, w1, ggate, ALU.mult))
                step(v.tensor_tensor(w2, w1, ex2, ALU.mult))
                step(v.tensor_tensor(gate, oh1, per_token(w1, 4), ALU.mult))
                step(v.tensor_tensor(gate2, oh2, per_token(w2, 4), ALU.mult))
                step(v.tensor_tensor(gate, gate, gate2, ALU.add))
                k = f"pos{l}"
                piece_in(dve, k)
                step(v.scalar_tensor_tensor(out=key, in0=pbank(k)[:, 0:8].rearrange("p (t g) -> p t g", t=TILES),
                                            scalar=1.0, in1=oh, op0=ALU.add, op1=ALU.mult))
                v.tensor_scalar(over, pbank(k)[:, 8:12], P + 0.5, None, ALU.is_gt).then_inc(evac[PIECES[k] % 2], 1)
                for t in range(TILES):
                    v.tensor_tensor(sel[:, t], slotno.unsqueeze(1).to_broadcast([P, GROUPS, P]),
                                    key[:, t].unsqueeze(2).to_broadcast([P, GROUPS, P]), ALU.is_equal).then_inc(sel_set, 1)
                piece_out(dve, k)
                step(v.tensor_reduce(ovn[:, 0:1], over, AX.X, ALU.add))
                step(v.tensor_tensor(ovd, over, first4[:, 0], ALU.mult))
                step(v.tensor_reduce(ovn[:, 1:2], ovd, AX.X, ALU.add))
                step(v.scalar_tensor_tensor(out=ovn[:, 1:2], in0=ovn[:, 0:1], scalar=4.0, in1=ovn[:, 1:2],
                                            op0=ALU.mult, op1=ALU.subtract))
                for t in range(TILES):
                    step(v.tensor_tensor(prod[:, t, 0], key[:, t], over, ALU.mult))
                step(v.tensor_reduce(key2, prod[:, :, 0], AX.X, ALU.add))
                step(v.tensor_scalar(key2, key2, float(P), None, ALU.subtract))
                v.tensor_copy(ovf[:, l, :], ovn).then_inc(ovf_set, 1)

            def experts(l):
                route(l)
                for c in range(CH):
                    k = PIECES[f"gather{l}{c}"]
                    if k % 2 == 0:
                        piece_in(dve, k)
                        v.tensor_scalar(xg[:, :, c, :], pbank(k).rearrange("p (g s) -> p g s", g=GROUPS),
                                        gffn[:, l, c:c + 1], None, ALU.mult).then_inc(evac[0], 1)
                for name, dst in ((f"gates{l}", None), (f"selT{l}0", two(selT[:, 0:2])), (f"selT{l}1", two(selT[:, 2:4]))):
                    if name[0] == "g":
                        evacuate(dve, False, name, two(gslot), src=pbank(name)[:, 0:GROUPS * EPG])
                    else:
                        evacuate(dve, False, name, dst)
                x0 = l * GROUPS * EPG
                for c in range(2):
                    piece_out(dve, PIECES[f"gather{l}7"] - c)
                piece_out(dve, f"gates{l}")

                def current(g):
                    v.tensor_scalar(gcur, gslot[:, g], 1.0, None, ALU.mult)
                    v.tensor_scalar(xcur.rearrange("p c s -> p (c s)"), xg[:, g].rearrange("p c s -> p (c s)"), 1.0,
                                    None, ALU.mult).then_inc(xcur_set, 1)

                def hidden(x, e, turns):
                    dve.wait_ge(up_ps, x + 1 + turns * EPG)
                    dve.wait_ge(silu_sb, x + 1 + turns * EPG)
                    v.scalar_tensor_tensor(out=hid.rearrange("p c f -> p f c"),
                                           in0=bank[1].rearrange("p (f c) -> p f c", c=FC), scalar=gcur[:, e:e + 1],
                                           in1=silu[:, e % 2, :].rearrange("p (f c) -> p f c", c=FC),
                                           op0=ALU.mult, op1=ALU.mult).then_inc(hid_sb, 1)

                def group_out(g, turns):
                    dve.wait_ge(y_ps, l * GROUPS + 1 + turns)
                    for f in range(2):
                        last = v.tensor_scalar(ysb[:, g, f * 512:(f + 1) * 512], bank[3 + f][:, :], 1.0, None, ALU.mult)
                    last.then_inc(y_free, 1)

                v.tensor_copy(tmp[:, :], gslot[:, 0:2, 0]).then_inc(y_free, 1)
                current(0)
                dve.wait_ge(xcur_set, l * GROUPS + 1)
                hidden(x0, 0, 0)
                with dve.Fori(0, GROUPS - 1) as g:
                    for e in range(1, EPG):
                        hidden(x0 + e, e, g)
                    dve.wait_ge(hid_sb, x0 + EPG + g * EPG)
                    current(g + 1)
                    dve.wait_ge(xcur_set, l * GROUPS + 2 + g)
                    hidden(x0 + EPG, 0, g)
                    group_out(g, g)
                for e in range(1, EPG):
                    hidden(x0 + e, e, GROUPS - 1)
                group_out(GROUPS - 1, GROUPS - 1)
                for i in range(4):
                    add((R_MOE0, R_MOE1)[l], i)
                second_pass(l)
                dve.wait_ge(resid, (R_MOE0, R_MOE1)[l] + 4)
                v.tensor_copy(tmp[:, :], h[:, :, 0]).then_inc(moe_done, 1)

            def second_pass(l):
                s = second[l]
                flag = dve.value_load(ovf[0:1, l, 0:1], min_val=0, max_val=1)
                with dve.If(flag > 0):
                    for t in range(TILES):
                        v.tensor_scalar(sel2[:, t], slotno, key2[:, t:t + 1], None, ALU.is_equal).then_inc(s["sel"], 1)
                    dve.wait_ge(s["parts"], 3)
                    v.tensor_copy(selT[:, 0, :], bank[0][:, 0:SEQ])
                    v.tensor_copy(gcur, bank[1][:, 0:EPG])
                    for c in range(CH):
                        last = v.tensor_scalar(xcur[:, c, :], bank[2 + c // 4][:, (c % 4) * P:(c % 4 + 1) * P],
                                               gffn[:, l, c:c + 1], None, ALU.mult)
                    last.then_inc(s["tokens"], 1)
                    dve.wait_ge(s["tokens"], 1)
                    v.memset(acc2, 0.0).then_inc(s["y_sb"], 1)
                    dve.wait_ge(s["y_sb"], 1)
                    with dve.Fori(0, EPG) as e:
                        dve.wait_ge(s["up_ps"], e + 1)
                        dve.wait_ge(s["silu"], e + 1)
                        v.scalar_tensor_tensor(out=hid.rearrange("p c f -> p f c"),
                                               in0=bank[1].rearrange("p (f c) -> p f c", c=FC), scalar=gcur[:, 0:1],
                                               in1=silu[:, 0, :].rearrange("p (f c) -> p f c", c=FC),
                                               op0=ALU.mult, op1=ALU.mult).then_inc(s["hid"], 1)
                        dve.wait_ge(s["hid"], e + 1)
                        for i in range(EPG - 1):
                            v.tensor_copy(gcur[:, i:i + 1], gcur[:, i + 1:i + 2]).then_inc(s["step"], 1)
                            dve.wait_ge(s["step"], e * (EPG - 1) + 1 + i)
                        dve.wait_ge(s["y_ps"], e + 1)
                        for f in range(2):
                            last = v.tensor_tensor(acc2[:, f * 512:(f + 1) * 512], bank[3 + f][:, :],
                                                   acc2[:, f * 512:(f + 1) * 512], ALU.add)
                        last.then_inc(s["y_sb"], 1)
                        dve.wait_ge(s["y_sb"], e + 2)
                    for i in range(4):
                        t, f = divmod(i, 2)
                        dve.wait_ge(s["proj"], i + 1)
                        r = h[:, t, f * 512:(f + 1) * 512]
                        v.tensor_tensor(r, scatter_bank(i)[:, :], r, ALU.add).then_inc(s["step"], 1)
                    dve.wait_ge(s["step"], EPG * (EPG - 1) + 4)

            cross(0)
            norm("3")
            experts(0)
            norm("4")

            def o_maxima(i, n, turns=0):
                dve.wait_ge(hb_in[n], 16 * (P // SKEW) * (i // 2 + 1) + turns * 16 * (P // SKEW))
                for g in range(CG):
                    dve.wait_ge(o_scores, CG * i + g + 1 + turns * 2 * CG)
                    for t in range(2):
                        last = v.scalar_tensor_tensor(out=op[:, g, t, :], in0=bank[(0, 1, 5)[g]][:, t * 256:(t + 1) * 256],
                                                      scalar=float(P) ** -0.5, in1=hb[:, n, g, P - t * P:P - t * P + 256],
                                                      op0=ALU.mult, op1=ALU.add)
                last.then_inc(o_logits, 1)
                dve.wait_ge(o_logits, i + 1 + turns * 2)
                v.tensor_reduce(negm[:, n, :], op.rearrange("p g t k -> p t g k"), AX.XY, ALU.max,
                                negate=True).then_inc(o_maxed, 1)

            def o_normalise(i, n, turns=0):
                dve.wait_ge(o_exped, i + 1 + turns * 2)
                v.reciprocal(rden[:, n, :], den[:, n, :]).then_inc(o_rden, 1)
                dve.wait_ge(o_rden, i + 1 + turns * 2)
                for t in range(2):
                    last = v.tensor_scalar(op[:, :, t, :], op[:, :, t, :], rden[:, n, t:t + 1], None, ALU.mult)
                last.then_inc(o_probs, 1)

            def o_head(i, nxt, turns=0):
                n = i % 2
                o_maxima(i, n, turns)
                for m in range(3):
                    if nxt:
                        odd_piece_out(dve, False, 5 * (i + 1) + m, turns, (i + 1) % 2)
                o_normalise(i, n, turns)
                if nxt:
                    odd_piece_out(dve, False, 5 * (i + 1) + 3, turns, (i + 1) % 2)
                dve.wait_ge(o_pv_ps, i + 1 + turns * 2)
                v.tensor_scalar(oyT[:, turns * 2 + i, :], bank[4][:, 0:SEQ], 1.0, None, ALU.mult).then_inc(o_pv_sb, 1)
                if nxt:
                    odd_piece_out(dve, False, 5 * (i + 1) + 4, turns, (i + 1) % 2)

            for m in range(5):
                odd_piece_out(dve, False, m, 0, 0)
            with dve.Fori(0, C_HEADS // 2 - 1) as j:
                for i in range(2):
                    o_head(i, True, j)
            o_head(C_HEADS - 2, True)
            o_head(C_HEADS - 1, False)
            norm("5")
            cross(1)
            norm("6")
            experts(1)
            norm("7")


INPUTS = ["x", "mem", "ln_mix", "ln_cross", "ln_mem", "ln_ffn", "ln_final", "rel_table", "even_w_in", "even_w_out",
          "sgu_ln_g", "sgu_ln_b", "sgu_w", "sgu_b", "attn_sink", "odd_w_in", "odd_w_out", "xq_w", "xkv_w", "xo_w",
          "router_group_w", "router_group_b", "router_expert_w", "router_expert_b",
          "expert_w_gate", "expert_w_up", "expert_w_down"]


def kernel(**inputs):
    import concourse.bacc as bacc
    from concourse.bass_utils import run_bass_kernel_spmd

    nc = bacc.Bacc("TRN2", target_bir_lowering=False, num_devices=1)
    arrays, args = {}, []
    shaped = {"consts": constants(), "selectors": bias_selectors().reshape(BUCKETS + 1, -1)}
    for name in INPUTS + list(shaped):
        a = np.ascontiguousarray(inputs[name] if name in inputs else shaped[name])
        arrays[name + "_in"] = a
        args.append(nc.dram_tensor(name + "_in", a.shape, mybir.dt.from_np(a.dtype), kind="ExternalInput").ap())
    out = nc.dram_tensor("out", (1, SEQ, D), F32, kind="ExternalOutput").ap()
    encoder(nc, *args, out)
    r = run_bass_kernel_spmd(nc, [arrays], core_ids=[0])
    return r.results[0]["out"]
```
